# Optimizing a Trainium2 kernel written in Bass

```python
import math
import jax, jax.numpy as jnp
from jax import lax
import numpy as np

D_MODEL = 1024
BATCH = 1
SEQ = 256
DEPTH = 1

CHUNK = 64
MIX_WIDTH = D_MODEL
ATT_WIDTH = D_MODEL // 2
HD = 64
N_Q = ATT_WIDTH // HD
N_KV = 2
GROUP = N_Q // N_KV
ML_WIDTH = MIX_WIDTH - ATT_WIDTH
ML_H = 4
ML_D = ML_WIDTH // ML_H
CONV_W = 4
ROPE_THETA = 10000.0
ATT_Q_W = N_Q * HD
ATT_KV_W = N_KV * HD
IN_SIZES = (ATT_Q_W, ATT_KV_W, ATT_KV_W, ML_WIDTH, ML_WIDTH, ML_WIDTH, ML_WIDTH, ML_H, ML_H)
IN_WIDTH = ATT_Q_W + 2 * ATT_KV_W + 4 * ML_WIDTH + 2 * ML_H
N_MEM = 256
MEM_HEADS = 4
MEM_HD = D_MODEL // MEM_HEADS
N_EXPERTS = 32
TOP_K = 4
D_FF = D_MODEL
SWIGLU_LIMIT = 7.0
SWIGLU_ALPHA = 1.702
MOE_BLOCK = 256
DEEPNORM_ALPHA = (2.0 * DEPTH) ** 0.25
DEEPNORM_BETA = (8.0 * DEPTH) ** -0.25
LN_EPS = 1e-5

kernel_name = 'hybrid_swa_mlstm_moe_encoder_layer'

def layer_norm(x, g, b):
    xf = x.astype(jnp.float32)
    mu = xf.mean(-1, keepdims=True)
    var = jnp.square(xf - mu).mean(-1, keepdims=True)
    y = (xf - mu) * lax.rsqrt(var + LN_EPS) * g.astype(jnp.float32) + b.astype(jnp.float32)
    return y.astype(x.dtype)

def rope_tables(seq, dtype):
    inv = 1.0 / (ROPE_THETA ** (jnp.arange(0, HD, 2, dtype=jnp.float32) / HD))
    ang = jnp.arange(seq, dtype=jnp.float32)[:, None] * inv[None, :]
    ang = jnp.concatenate([ang, ang], axis=-1)
    return jnp.cos(ang).astype(dtype), jnp.sin(ang).astype(dtype)

def apply_rope(t, cos, sin):
    t1, t2 = t[..., : HD // 2], t[..., HD // 2:]
    rot = jnp.concatenate([-t2, t1], axis=-1)
    return t * cos[None, :, None, :] + rot * sin[None, :, None, :]

def sliding_window_sink_attention(q, k, v, sinks):
    B, S = q.shape[:2]
    nc = S // CHUNK
    qc = q.reshape(B, nc, CHUNK, N_KV, GROUP, HD)
    kc = k.reshape(B, nc, CHUNK, N_KV, HD)
    vc = v.reshape(B, nc, CHUNK, N_KV, HD)
    pad = jnp.zeros((B, 1, CHUNK, N_KV, HD), k.dtype)
    kb = jnp.concatenate([jnp.concatenate([pad, kc[:, :-1]], axis=1), kc], axis=2)
    vb = jnp.concatenate([jnp.concatenate([pad, vc[:, :-1]], axis=1), vc], axis=2)
    s = jnp.einsum('bcqhgd,bckhd->bchgqk', qc, kb).astype(jnp.float32) * (HD ** -0.5)
    kidx = jnp.arange(2 * CHUNK)[None, :]
    valid = (kidx >= CHUNK) | (jnp.arange(nc)[:, None] > 0)
    s = jnp.where(valid[None, :, None, None, None, :], s, -jnp.inf)
    sink = sinks.astype(jnp.float32).reshape(N_KV, GROUP)[None, None, :, :, None, None]
    m = jnp.maximum(s.max(-1, keepdims=True), sink)
    p = jnp.exp(s - m)
    p = p / (p.sum(-1, keepdims=True) + jnp.exp(sink - m))
    o = jnp.einsum('bchgqk,bckhd->bcqhgd', p.astype(v.dtype), vb)
    return o.reshape(B, S, N_Q * HD)

def mlstm_chunkwise(q, k, v, ig, lf):
    B, S, H, DK = q.shape
    DV = v.shape[-1]
    nc = S // CHUNK

    def to_chunks(t):
        return jnp.moveaxis(t.reshape((B, nc, CHUNK) + t.shape[2:]), 1, 0)

    causal = jnp.tril(jnp.ones((CHUNK, CHUNK), bool))[None, :, :, None]

    def step(carry, xs):
        c_state, n_state, m_state = carry
        qc, kc, vc, ic, fc = xs
        b = jnp.cumsum(fc, axis=1)
        b_end = b[:, -1]
        d = jnp.where(causal, b[:, :, None, :] - b[:, None, :, :] + ic[:, None, :, :], -jnp.inf)
        inter = b + m_state[:, None, :]
        m_t = jnp.maximum(inter, d.max(axis=2))
        w_intra = jnp.einsum('bthd,bshd->btsh', qc, kc) * jnp.exp(d - m_t[:, :, None, :])
        w_inter = jnp.exp(inter - m_t)
        num = (jnp.einsum('btsh,bshv->bthv', w_intra, vc)
               + w_inter[..., None] * jnp.einsum('bthd,bhdv->bthv', qc, c_state))
        den = w_intra.sum(axis=2) + w_inter * jnp.einsum('bthd,bhd->bth', qc, n_state)
        h = num / jnp.maximum(jnp.abs(den), jnp.exp(-m_t))[..., None]
        w_src = b_end[:, None, :] - b + ic
        m_new = jnp.maximum(b_end + m_state, w_src.max(axis=1))
        decay = jnp.exp(b_end + m_state - m_new)
        w_k = jnp.exp(w_src - m_new[:, None, :])
        c_new = decay[..., None, None] * c_state + jnp.einsum('bsh,bshd,bshv->bhdv', w_k, kc, vc)
        n_new = decay[..., None] * n_state + jnp.einsum('bsh,bshd->bhd', w_k, kc)
        return (c_new, n_new, m_new), h

    init = (jnp.zeros((B, H, DK, DV), jnp.float32), jnp.zeros((B, H, DK), jnp.float32),
            jnp.zeros((B, H), jnp.float32))
    _, h = lax.scan(step, init, tuple(to_chunks(t) for t in (q, k, v, ig, lf)))
    return jnp.moveaxis(h, 0, 1).reshape(B, S, H, DV)

def causal_conv_silu(t, w, b):
    S = t.shape[1]
    tp = jnp.pad(t, ((0, 0), (CONV_W - 1, 0), (0, 0)))
    y = b + sum(tp[:, j:j + S] * w[j] for j in range(CONV_W))
    return jax.nn.silu(y)

def hybrid_mixer(x, w_in, conv_w, conv_b, attn_sinks, b_igate, b_fgate, mlstm_norm_w, w_out):
    B, S, _ = x.shape
    proj = x @ w_in
    offs, acc = [], 0
    for s in IN_SIZES[:-1]:
        acc += s
        offs.append(acc)
    aq, ak, av, mq, mk, mv, mo, mi, mf = jnp.split(proj, offs, axis=-1)
    cos, sin = rope_tables(S, x.dtype)
    aq = apply_rope(aq.reshape(B, S, N_Q, HD), cos, sin)
    ak = apply_rope(ak.reshape(B, S, N_KV, HD), cos, sin)
    att = sliding_window_sink_attention(aq, ak, av.reshape(B, S, N_KV, HD), attn_sinks)
    qk = causal_conv_silu(jnp.concatenate([mq, mk], axis=-1), conv_w, conv_b)
    mq, mk = qk[..., :ML_WIDTH], qk[..., ML_WIDTH:]
    f32 = jnp.float32
    hm = mlstm_chunkwise(
        mq.reshape(B, S, ML_H, ML_D).astype(f32) * (ML_D ** -0.5),
        mk.reshape(B, S, ML_H, ML_D).astype(f32),
        mv.reshape(B, S, ML_H, ML_D).astype(f32),
        (mi + b_igate).astype(f32),
        jax.nn.log_sigmoid((mf + b_fgate).astype(f32)))
    mu = hm.mean(-1, keepdims=True)
    var = jnp.square(hm - mu).mean(-1, keepdims=True)
    hm = (hm - mu) * lax.rsqrt(var + LN_EPS) * mlstm_norm_w.astype(f32).reshape(ML_H, ML_D)
    hm = (jax.nn.sigmoid(mo.reshape(B, S, ML_H, ML_D).astype(f32)) * hm).astype(x.dtype)
    return jnp.concatenate([att, hm.reshape(B, S, ML_WIDTH)], axis=-1) @ w_out

def memory_cross_attention(x, mem, w_cq, w_ck, w_cv, w_co):
    B, S, _ = x.shape
    q = (x @ w_cq).reshape(B, S, MEM_HEADS, MEM_HD)
    k = (mem @ w_ck).reshape(B, -1, MEM_HEADS, MEM_HD)
    v = (mem @ w_cv).reshape(B, -1, MEM_HEADS, MEM_HD)
    s = jnp.einsum('bshd,bmhd->bhsm', q, k).astype(jnp.float32) * (MEM_HD ** -0.5)
    p = jax.nn.softmax(s, axis=-1).astype(v.dtype)
    o = jnp.einsum('bhsm,bmhd->bshd', p, v).reshape(B, S, D_MODEL)
    return o @ w_co

def moe_ffn(x2, w_router, b_router, w_gu, b_gu, w_down, b_down):
    T = x2.shape[0]
    logits = (x2 @ w_router + b_router).astype(jnp.float32)
    top_vals, top_idx = lax.top_k(logits, TOP_K)
    gates = jax.nn.softmax(top_vals, axis=-1).astype(x2.dtype)
    flat_e = top_idx.reshape(-1)
    flat_tok = jnp.arange(T * TOP_K, dtype=jnp.int32) // TOP_K
    flat_g = gates.reshape(-1)
    order = jnp.argsort(flat_e)
    e_sorted = flat_e[order]
    counts = jnp.bincount(flat_e, length=N_EXPERTS)
    padded = ((counts + MOE_BLOCK - 1) // MOE_BLOCK) * MOE_BLOCK
    start = jnp.cumsum(counts) - counts
    pend = jnp.cumsum(padded)
    pstart = pend - padded
    dest = pstart[e_sorted] + (jnp.arange(T * TOP_K) - start[e_sorted])
    n_rows = T * TOP_K + N_EXPERTS * MOE_BLOCK
    n_blocks = n_rows // MOE_BLOCK
    row_tok = jnp.zeros((n_rows,), jnp.int32).at[dest].set(flat_tok[order])
    row_gate = jnp.zeros((n_rows,), x2.dtype).at[dest].set(flat_g[order])
    block_e = jnp.minimum(jnp.searchsorted(pend, jnp.arange(n_blocks) * MOE_BLOCK, side='right'),
                          N_EXPERTS - 1)

    def expert_block(args):
        tok, e = args
        h = x2[tok] @ w_gu[e] + b_gu[e]
        g = jnp.minimum(h[:, :D_FF], SWIGLU_LIMIT)
        u = jnp.clip(h[:, D_FF:], -SWIGLU_LIMIT, SWIGLU_LIMIT)
        y = (u + 1.0) * (g * jax.nn.sigmoid(SWIGLU_ALPHA * g))
        return y @ w_down[e] + b_down[e]

    y_rows = lax.map(expert_block, (row_tok.reshape(n_blocks, MOE_BLOCK), block_e))
    y_rows = y_rows.reshape(n_rows, -1) * row_gate[:, None]
    return jnp.zeros_like(x2).at[row_tok].add(y_rows)

def setup_inputs(seed: int = 0) -> dict:
    key = jax.random.key(seed)
    ks = iter(jax.random.split(key, 32))
    nrm = lambda shape: jax.random.normal(next(ks), shape, jnp.float32)
    L = DEPTH
    beta = DEEPNORM_BETA
    col_scale = np.concatenate([
        np.ones(ATT_Q_W + ATT_KV_W), np.full(ATT_KV_W, beta),
        np.ones(2 * ML_WIDTH), np.full(ML_WIDTH, beta), np.ones(ML_WIDTH + 2 * ML_H)]).astype(np.float32)
    return {
        'x': nrm((BATCH, SEQ, D_MODEL)),
        'mem': nrm((BATCH, N_MEM, D_MODEL)),
        'w_in': nrm((L, D_MODEL, IN_WIDTH)) * (D_MODEL ** -0.5) * jnp.asarray(col_scale),
        'conv_w': nrm((L, CONV_W, 2 * ML_WIDTH)) * (CONV_W ** -0.5),
        'conv_b': 0.02 * nrm((L, 2 * ML_WIDTH)),
        'attn_sinks': 0.5 * nrm((L, N_Q)),
        'b_igate': 0.1 * nrm((L, ML_H)),
        'b_fgate': jnp.linspace(3.0, 6.0, ML_H)[None, :] + 0.1 * nrm((L, ML_H)),
        'mlstm_norm_w': 1.0 + 0.02 * nrm((L, ML_WIDTH)),
        'w_out': nrm((L, MIX_WIDTH, D_MODEL)) * (MIX_WIDTH ** -0.5) * beta,
        'ln1_g': 1.0 + 0.02 * nrm((L, D_MODEL)),
        'ln1_b': 0.02 * nrm((L, D_MODEL)),
        'w_cq': nrm((L, D_MODEL, D_MODEL)) * (D_MODEL ** -0.5),
        'w_ck': nrm((L, D_MODEL, D_MODEL)) * (D_MODEL ** -0.5),
        'w_cv': nrm((L, D_MODEL, D_MODEL)) * (D_MODEL ** -0.5) * beta,
        'w_co': nrm((L, D_MODEL, D_MODEL)) * (D_MODEL ** -0.5) * beta,
        'ln2_g': 1.0 + 0.02 * nrm((L, D_MODEL)),
        'ln2_b': 0.02 * nrm((L, D_MODEL)),
        'w_router': nrm((L, D_MODEL, N_EXPERTS)) * (D_MODEL ** -0.5),
        'b_router': 0.01 * nrm((L, N_EXPERTS)),
        'w_gu': nrm((L, N_EXPERTS, D_MODEL, 2 * D_FF)) * (D_MODEL ** -0.5) * beta,
        'b_gu': 0.02 * nrm((L, N_EXPERTS, 2 * D_FF)),
        'w_down': nrm((L, N_EXPERTS, D_FF, D_MODEL)) * (D_FF ** -0.5) * beta,
        'b_down': 0.02 * nrm((L, N_EXPERTS, D_MODEL)),
        'ln3_g': 1.0 + 0.02 * nrm((L, D_MODEL)),
        'ln3_b': 0.02 * nrm((L, D_MODEL)),
    }

def reference(x, mem, w_in, conv_w, conv_b, attn_sinks, b_igate, b_fgate, mlstm_norm_w, w_out,
              ln1_g, ln1_b, w_cq, w_ck, w_cv, w_co, ln2_g, ln2_b,
              w_router, b_router, w_gu, b_gu, w_down, b_down, ln3_g, ln3_b):
    B, S, D = x.shape
    h = x
    for l in range(DEPTH):
        mix = hybrid_mixer(h, w_in[l], conv_w[l], conv_b[l], attn_sinks[l], b_igate[l], b_fgate[l],
                           mlstm_norm_w[l], w_out[l])
        h = layer_norm(DEEPNORM_ALPHA * h + mix, ln1_g[l], ln1_b[l])
        ca = memory_cross_attention(h, mem, w_cq[l], w_ck[l], w_cv[l], w_co[l])
        h = layer_norm(DEEPNORM_ALPHA * h + ca, ln2_g[l], ln2_b[l])
        ff = moe_ffn(h.reshape(B * S, D), w_router[l], b_router[l], w_gu[l], b_gu[l],
                     w_down[l], b_down[l]).reshape(B, S, D)
        h = layer_norm(DEEPNORM_ALPHA * h + ff, ln3_g[l], ln3_b[l])
    return h


_drawn_inputs = setup_inputs


def setup_inputs(seed=0):
    import zlib

    import numpy as np

    out = dict(_drawn_inputs(seed))
    spreads = {}
    factors = {'conv_b': 8.0,
     'attn_sinks': 56.068,
     'b_igate': 64.0,
     'mlstm_norm_w': 23.522,
     'b_router': 7.414,
     'b_gu': 8.0,
     'b_down': 6.277,
     'ln3_g': 8.03,
     'ln3_b': 7.986}
    for name, (base, spread) in spreads.items():
        noise = np.random.default_rng([zlib.crc32(name.encode()), seed]).standard_normal(out[name].shape)
        drawn = base * np.exp(spread * noise) if base else spread * noise
        out[name] = __import__('jax').numpy.asarray(drawn.astype(out[name].dtype))
    for name, factor in factors.items():
        out[name] = (out[name] * factor).astype(out[name].dtype)
    return out
```

```python
from contextlib import ExitStack

import concourse.bass as bass
from concourse import mybir

F32 = mybir.dt.float32
BF16 = mybir.dt.bfloat16
I32 = mybir.dt.int32
U32 = mybir.dt.uint32
ALU = mybir.AluOpType
ACT = mybir.ActivationFunctionType
AX_X = mybir.AxisListType.X

P = 128

D = 1024
SEQ = 256
TT = SEQ // P
KT = D // P
CHUNK = 64
NCHUNK = SEQ // CHUNK
HD = 64
N_Q = 8
N_KV = 2
GROUP = N_Q // N_KV
ML_W = 512
ML_H = 4
CONV_W = 4
N_MEM = 256
MEM_H = 4
MEM_HD = D // MEM_H
N_EXP = 32
TOP_K = 4
D_FF = 1024
LIMIT = 7.0
SWIGLU_ALPHA = 1.702
DEEPNORM_ALPHA = 2.0 ** 0.25
LN_EPS = 1e-5
BIG = 1.0e30

C_AQ, C_AK, C_AV, C_MQ, C_MK, C_MV, C_MO, C_GATE = 0, 512, 640, 768, 1280, 1792, 2304, 2816

SLOTS = 64
MAX_PASSES = N_EXP + (SEQ * TOP_K) // (SLOTS + 1)
EXP_CHUNKS = 6
UNROLL = 3
LOOPS = N_EXP // UNROLL

SLOT = 4096
RING = 9
FRONT_SLOTS = 6
PIECES = ["mq", "mk", "mo", "mv", "akav", "aq", "ck0", "ck1", "wo0", "wo1", "cv0", "cv1", "cq0", "cq1", "co0", "co1"]
RING_ORDER = [6, 7, 4, 5, 0, 1, 2, 3, 8]

E_TRI, E_ROT, E_COS, E_SIN, E_NEG, E_POS, E_PAR = 0, 128, 256, 512, 768, 896, 1024
E_W = 1024 + 8 + 8 + ML_W
L_ID, L_STRICT, L_IOTA, L_ESTRICT, L_EINCL, L_ROWS, L_W = 0, 128, 256, 320, 352, 384, 640


def front_slot(piece):
    n = PIECES.index(piece)
    return n % FRONT_SLOTS, n // FRONT_SLOTS + 1


def layer_program(nc, x, xT, memT, w_in, conv_p, early, early_par, late, w_out, ln_p, w_cq, w_ck, w_cv, w_co,
                  w_router, b_router, w_gu, b_gu, w_down, b_down, out):
    with ExitStack() as ctx:
        def sb(name, shape, dt=F32):
            return ctx.enter_context(nc.sbuf_tensor(name, shape, dt))

        def sem(name):
            return ctx.enter_context(nc.semaphore(name))

        X_W = KT * (CHUNK + SEQ)
        ring = sb("ring", [P, (RING - 1) * SLOT + X_W + 2048])
        xT_sb = ring[:, (RING - 1) * SLOT:(RING - 1) * SLOT + X_W]
        ebuf = ring[:, (RING - 1) * SLOT + X_W:]
        XROWS = RING * SLOT - ((RING - 1) * SLOT + X_W)
        res = sb("res", [P, TT, D])
        memT_sb = sb("memT_sb", [P, KT, N_MEM])
        memK = sb("memK", [P, KT, N_MEM])
        memV = sb("memV", [P, 2, D])
        qbuf = sb("qbuf", [P, 2048])
        akT = sb("akT", [P, CHUNK + SEQ])
        akrot = sb("akrot", [P, SEQ])
        lnp = sb("lnp", [P, 2048])
        late_c = sb("late_c", [P, L_W])
        ones = sb("ones", [P, P])
        router_w = sb("router_w", [P, KT, N_EXP])
        brow = sb("brow", [P, N_EXP])
        convp = sb("convp", [P, 8, CONV_W + 1])
        gate_w = sb("gate_w", [P, KT, 8])
        bgu3 = sb("bgu3", [P, 2 * D_FF], BF16)
        sm = sb("sm", [P, 400])

        psum = [ctx.enter_context(nc.psum_tensor(f"bank{i}", [P, 512], F32)) for i in range(8)]

        def slot_words(i):
            return ring[:, i * SLOT:(i + 1) * SLOT]

        xT_pad = xT_sb.rearrange("p (k t) -> p k t", k=KT)
        xk = xT_pad[:, :, CHUNK:]
        tT = xT_sb[:, 0:KT * SEQ].rearrange("p (k t) -> p k t", k=KT)
        aqT = qbuf[:, 0:1024].rearrange("p (m t) -> p m t", m=4)
        mqT = qbuf[:, 1024:2048].rearrange("p (m t) -> p m t", m=4)
        hm = qbuf[:, 1024:2048].rearrange("p (t h d) -> p t h d", t=TT, h=ML_H)
        cqT = qbuf[:].rearrange("p (m t) -> p m t", m=8)
        decay = ebuf[:, 0:1536].rearrange("p (b h t) -> p b h t", b=3, h=ML_H)
        av = ebuf[:, 1536:2048].rearrange("p (c d) -> p c d", c=4)
        cPT = ebuf.rearrange("p (m h t) -> p m h t", m=2, h=MEM_H)
        cP = memT_sb[:].rearrange("p k t -> p (k t)").rearrange("p (h t m) -> p h t m", h=MEM_H, t=TT)
        S6 = slot_words(6)
        S7 = slot_words(7)
        sigq = S6[:, 0:2048].rearrange("p (m t) -> p m t", m=8)
        prob = S6[:, 0:2048].rearrange("p (t h k) -> p t h k", t=TT, h=N_Q)
        probT = S6[:, 2048:4096].rearrange("p (t h q) -> p t h q", t=TT, h=N_Q)
        diag = S6[:, 2048:3072].rearrange("p (t h s) -> p t h s", t=TT, h=ML_H)
        qrot = S6[:, 3072:4096].rearrange("p (m t) -> p m t", m=4)
        mkT = S7[:, 0:1024].rearrange("p (m t) -> p m t", m=4)
        mv1 = S7[:, 1024:2056].rearrange("p (t h d) -> p t h d", t=TT, h=ML_H)
        sigo = S7[:, 2056:3080].rearrange("p (t n) -> p t n", t=TT)
        early_c = lnp[:, 0:E_W]
        tri, rot = early_c[:, E_TRI:E_TRI + P], early_c[:, E_ROT:E_ROT + P]
        cosT, sinT = early_c[:, E_COS:E_COS + SEQ], early_c[:, E_SIN:E_SIN + SEQ]
        negm, posm = early_c[:, E_NEG:E_NEG + P], early_c[:, E_POS:E_POS + P]
        sinks, bgate, normw = (early_c[:, E_PAR:E_PAR + 8], early_c[:, E_PAR + 8:E_PAR + 16],
                               early_c[:, E_PAR + 16:E_PAR + 16 + ML_W])
        ident = late_c[:, L_ID:L_ID + P]
        strict = late_c[:, L_STRICT:L_STRICT + P]
        iota = late_c[:, L_IOTA:L_IOTA + SLOTS]
        e_rows = late_c[0:N_EXP, L_ROWS:L_ROWS + 2 * P].rearrange("p (i m) -> p i m", i=2)
        e_both = late_c[0:N_EXP, L_ESTRICT:L_ESTRICT + 2 * N_EXP]
        bgu_raw = memK[:].rearrange("p k t -> p (k t)")
        bgu_rest = memV[:].rearrange("p k t -> p (k t)")
        m0 = memT_sb[:].rearrange("p k t -> p (k t)")
        k0 = memK[:].rearrange("p k t -> p (k t)")
        v0 = memV[:].rearrange("p k t -> p (k t)")
        xg = m0[:, 0:512].rearrange("p (c h s) -> p h c s", c=4, h=2)
        xrows = ebuf[:, XROWS:XROWS + 512]
        eq = m0[:, 512:1024].rearrange("p (t k s) -> p t k s", t=TT, k=TOP_K)
        gq = m0[:, 1024:1536].rearrange("p (t k s) -> p t k s", t=TT, k=TOP_K)
        hot = m0[:, 1536:1664].rearrange("p (t s) -> p t s", t=TT)
        hotg = m0[:, 1664:1920].rearrange("p (t f s) -> p t f s", t=TT, f=2)
        gcl = k0[:, 0:512]
        ucl = k0[:, 512:1024]
        sgm = k0[:, 1024:1536]
        scatT = k0[:, 1536:1792]
        act = v0[:, 0:512]
        actT = v0[:, 512:1024]
        ysb = v0[:, 1024:2048]
        bdown = ebuf[0:N_EXP, 0:D]
        gT = ebuf[0:N_EXP, 1024:1024 + SEQ].rearrange("p (t n) -> p t n", t=TT)
        logits = qbuf[:, 0:64].rearrange("p (t e) -> p t e", t=TT)
        top8 = qbuf[:, 64:80].rearrange("p (t k) -> p t k", t=TT)
        idx8 = qbuf[:, 80:96].bitcast(U32).rearrange("p (t k) -> p t k", t=TT)
        idx4 = qbuf[:, 96:104]
        eg = qbuf[:, 104:112].rearrange("p (t k) -> p t k", t=TT)
        gate = qbuf[:, 112:120]
        onehot = qbuf[:, 128:384].rearrange("p (j e) -> p j e", j=8)
        tmp8 = qbuf[:, 384:640].rearrange("p (j e) -> p j e", j=8)
        selm = qbuf[:, 640:704].rearrange("p (t e) -> p t e", t=TT)
        gfull = qbuf[:, 704:768].rearrange("p (t e) -> p t e", t=TT)
        dest = qbuf[:, 768:832].rearrange("p (t e) -> p t e", t=TT)
        rel = qbuf[:, 832:840]
        npass = qbuf[:, 840:841]
        first = qbuf[:, 841:842]
        last = qbuf[:, 842:843]
        began = qbuf[:, 843:844]
        steps = qbuf[:, 844:848]
        cumrow = qbuf[:, 848:912]
        osel = qbuf[:, 912:913].bitcast(BF16)[:, 0:1]
        npass_i = qbuf[:, 920:952].bitcast(I32)
        cum_i = qbuf[:, 952:984].bitcast(I32)
        rmax = qbuf[:, 984:986]
        rsum = qbuf[:, 986:988]

        gi = sm[:, 0:16].rearrange("p (t g) -> p t g", t=TT)
        gneg = sm[:, 16:24].rearrange("p (t h) -> p t h", t=TT)
        gln = sm[:, 24:32].rearrange("p (t h) -> p t h", t=TT)
        logf = sm[:, 32:40].rearrange("p (t h) -> p t h", t=TT)
        cumf = sm[:, 40:48].rearrange("p (t h) -> p t h", t=TT)
        csrc = sm[:, 48:56].rearrange("p (t h) -> p t h", t=TT)
        mrun = sm[:, 56:64].rearrange("p (t h) -> p t h", t=TT)
        m3 = sm[:, 64:76].rearrange("p (b h) -> p b h", b=3)
        fm = sm[:, 76:84].rearrange("p (t h) -> p t h", t=TT)
        dmin = sm[:, 84:92].rearrange("p (t h) -> p t h", t=TT)
        den = sm[:, 92:100].rearrange("p (t h) -> p t h", t=TT)
        hst = sm[:, 100:148].rearrange("p (j s) -> p j s", j=8)
        hag = sm[:, 148:164].rearrange("p (j s) -> p j s", j=8)
        hrs = sm[:, 164:172]
        amax = sm[:, 172:188].rearrange("p (t h) -> p t h", t=TT)
        asum = sm[:, 188:204].rearrange("p (t h) -> p t h", t=TT)
        asnk = sm[:, 204:220].rearrange("p (t h) -> p t h", t=TT)
        lst = sm[:, 220:244].rearrange("p (t c s) -> p t c s", t=TT, c=2)
        lag = sm[:, 244:248].rearrange("p (t s) -> p t s", t=TT)
        lrs = sm[:, 248:250]
        cmax = sm[:, 250:258]
        csum = sm[:, 258:266]
        lnt = sm[:, 266:282]
        nwt = sm[:, 282:298]
        epsc = sm[:, 298:299]

        slot_landed = [sem(f"slot_landed{i}") for i in range(RING)]
        mixer_done = sem("mixer_done")
        x_landed, xT_landed, memT_landed = sem("x_landed"), sem("xT_landed"), sem("memT_landed")
        early_landed, par_landed, late_landed = sem("early_landed"), sem("par_landed"), sem("late_landed")
        conv_landed, gatew_landed, bgu_landed = sem("conv_landed"), sem("gatew_landed"), sem("bgu_landed")
        router_landed, ln_landed, bdown_landed = sem("router_landed"), sem("ln_landed"), sem("bdown_landed")
        zero_done = sem("zero_done")
        pair_ready = [sem("pair_ready0"), sem("pair_ready1")]
        gates_ready, cum_ready, logf_ready = sem("gates_ready"), sem("cum_ready"), sem("logf_ready")
        exp1, ln1s = sem("exp1"), sem("ln1s")
        diag_ready, crow_ready, mdiag_ready, mrow_ready = sem("diag_ready"), sem("crow_ready"), sem("mdiag_ready"), sem("mrow_ready")
        decay_ready, sraw_ready, wts_ready, num_ready = sem("decay_ready"), sem("sraw_ready"), sem("wts_ready"), sem("num_ready")
        sig_ready, qk_ready = sem("sig_ready"), sem("qk_ready")
        fm_ready, dmin_ready, hvar_ready, hln_ready, hm_ready = sem("fm_ready"), sem("dmin_ready"), sem("hvar_ready"), sem("hln_ready"), sem("hm_ready")
        rope_ready = sem("rope_ready")
        sco_ready, sco_read, pmax_ready, pexp_ready, prob_ready = sem("sco_ready"), sem("sco_read"), sem("pmax_ready"), sem("pexp_ready"), sem("prob_ready")
        pT_ready, pT_read = sem("pT_ready"), sem("pT_read")
        var_ready, lnlog_ready, normed = sem("var_ready"), sem("lnlog_ready"), sem("normed")
        cs_ready, cmax_ready, cexp_ready, cprob_ready, cpT_ready, cpT_read = (sem("cs_ready"), sem("cmax_ready"), sem("cexp_ready"),
                                                                           sem("cprob_ready"), sem("cpT_ready"), sem("cpT_read"))
        bgu_split = sem("bgu_split")
        rmax_ready, rexp_ready, sel_ready, rank_ready = sem("rmax_ready"), sem("rexp_ready"), sem("sel_ready"), sem("rank_ready")
        npass_ready, base_ready, gT_ready, gT_read, tables_ready = sem("npass_ready"), sem("base_ready"), sem("gT_ready"), sem("gT_read"), sem("tables_ready")
        chunk_used = [sem(f"chunk_used{c}") for c in range(EXP_CHUNKS)]
        hot_ready, hotg_ready, gath_done, xg_ready = sem("hot_ready"), sem("hotg_ready"), sem("gath_done"), sem("xg_ready")
        gcl_ready, sgm_ready, act_ready = sem("gcl_ready"), sem("sgm_ready"), sem("act_ready")
        scT_done, scT_ready, aT_done, aT_ready = sem("scT_done"), sem("scT_ready"), sem("aT_done"), sem("aT_ready")
        sums_open, y0_ready, y1_ready, scattered = sem("sums_open"), sem("y0_ready"), sem("y1_ready"), sem("scattered")
        xrows_ready, xgT_done = sem("xrows_ready"), sem("xgT_done")
        num_read, sum_ready, tail_step = sem("num_read"), sem("sum_ready"), sem("tail_step")
        dve_step, act_step, pool_step = sem("dve_step"), sem("act_step"), sem("pool_step")
        stored, final_ready = sem("stored"), sem("final_ready")

        def columns(w, c0, n):
            return w[:, c0:c0 + n].rearrange("(k p) n -> p k n", p=P)

        def slot_view(s, n):
            return slot_words(s)[:, 0:KT * n].rearrange("p (k n) -> p k n", k=KT)

        SOURCE = {"mq": (w_in, C_MQ, 512), "mk": (w_in, C_MK, 512), "mo": (w_in, C_MO, 512), "mv": (w_in, C_MV, 512),
                  "akav": (w_in, C_AK, 256), "aq": (w_in, C_AQ, 512)}
        for nm, w in (("ck", w_ck), ("wo", w_out), ("cv", w_cv), ("cq", w_cq), ("co", w_co)):
            for i in range(2):
                SOURCE[f"{nm}{i}"] = (w, 512 * i, 512)

        gu_rows = w_gu.rearrange("e (c j p) n -> e c p j n", p=P, j=2)
        down_cols = w_down.rearrange("e (k p) (c n) -> e c p k n", p=P, c=2)

        front_loads = [len(range(s, len(PIECES), FRONT_SLOTS)) if s < FRONT_SLOTS else 0 for s in range(RING)]

        UNITS = ["mq", "mk", "mo", "mv", "akav", "aq", "rotq", "rotk", "ck0", "ck1", "hmT", "pv", "wo0", "wo1",
                 "cv0", "cv1", "x1T0", "x1T1", "cq0", "cq1", "oT0", "oT1", "co_t0", "co_t1", "x2T0", "x2T1", "logit"]
        PAIR_COUNT = {u: (i % 2, i // 2 + 1) for i, u in enumerate(UNITS)}
        TAKES = {u: {"mq": 4, "mk": 4, "rotk": 1, "logit": 1}.get(u, 2) for u in UNITS}
        taken = {u: sem(f"taken_{u}") for u in UNITS}

        def unit_banks(u):
            p_ = PAIR_COUNT[u][0]
            return psum[2 * p_], psum[2 * p_ + 1]

        def wait_unit(eng, u):
            eng.wait_ge(pair_ready[PAIR_COUNT[u][0]], PAIR_COUNT[u][1])

        def wait_piece_used(eng, piece):
            wait_unit(eng, "co_t1" if piece in ("co0", "co1") else piece)

        def wait_taken(eng, u):
            eng.wait_ge(taken[u], TAKES[u])

        block = ctx.enter_context(nc.Block())

        @block.sync
        def _(sp):
            sp.dma_start(gate_w[:], columns(w_in, C_GATE, 8)).then_inc(gatew_landed, 16)
            sp.dma_start(xk, xT.rearrange("(k p) t -> p k t", p=P)).then_inc(xT_landed, 16)
            for n, piece in enumerate(PIECES):
                if n >= FRONT_SLOTS:
                    wait_piece_used(sp, PIECES[n - FRONT_SLOTS])
                w, c0, width = SOURCE[piece]
                s, _ = front_slot(piece)
                sp.dma_start(slot_view(s, width), columns(w, c0, width)).then_inc(slot_landed[s], 16)
                if n == 3:
                    sp.dma_start(memT_sb[:], memT.rearrange("(k p) t -> p k t", p=P)).then_inc(memT_landed, 16)

            def load_chunk(e, c, n):
                s = RING_ORDER[n % RING]
                if c < 4:
                    src = gu_rows[e, c] if isinstance(e, int) else gu_rows[bass.ds(e, 1), c].rearrange("o p j n -> (o p) j n")
                    dst = slot_words(s).rearrange("p (j n) -> p j n", j=2)
                else:
                    src = down_cols[e, 5 - c] if isinstance(e, int) else down_cols[bass.ds(e, 1), 5 - c].rearrange("o p k n -> (o p) k n")
                    dst = slot_words(s).rearrange("p (k n) -> p k n", k=KT)
                sp.dma_start(dst, src).then_inc(slot_landed[s], 16)

            for n in range(UNROLL * EXP_CHUNKS):
                s = RING_ORDER[n % RING]
                e, c = divmod(n, EXP_CHUNKS)
                if n < RING:
                    if s < FRONT_SLOTS:
                        wait_piece_used(sp, PIECES[max(i for i in range(len(PIECES)) if i % FRONT_SLOTS == s)])
                    elif s < RING - 1:
                        sp.wait_ge(mixer_done, 1)
                    else:
                        sp.wait_ge(sums_open, 1)
                else:
                    if n == RING:
                        sp.wait_ge(tables_ready, 1)
                    pe_, pc_ = divmod(n - RING, EXP_CHUNKS)
                    sp.wait_ge(chunk_used[pc_], sp.value_load(cum_i[0:1, pe_:pe_ + 1], min_val=1, max_val=MAX_PASSES))
                load_chunk(e, c, n)

            def load_later(e0, chunks):
                before = [divmod(n + UNROLL * EXP_CHUNKS - RING, EXP_CHUNKS) for n in range(chunks)]
                passes_till = {pu: sp.value_load(cum_i[0:1, bass.ds(e0 + (pu - UNROLL), 1)], min_val=1, max_val=MAX_PASSES)
                               for pu in sorted({pu for pu, _ in before})}
                for n, (pu, pc_) in enumerate(before):
                    sp.wait_ge(chunk_used[pc_], passes_till[pu])
                    sp.nop(nofuse=True)
                    load_chunk(e0 + n // EXP_CHUNKS, n % EXP_CHUNKS, n)

            with sp.Fori(1, LOOPS) as it:
                load_later(it * UNROLL, UNROLL * EXP_CHUNKS)
            load_later(LOOPS * UNROLL, (N_EXP % UNROLL) * EXP_CHUNKS)
            for t in range(TT):
                sp.wait_ge(final_ready, t + 1)
                sp.dma_start(out[t * P:(t + 1) * P, :], res[:, t, :]).then_inc(stored, 16)
            sp.wait_ge(stored, 16 * TT)

        @block.gpsimd
        def _(pool):
            steps_done = [0]

            def link(ins):
                steps_done[0] += 1
                ins.then_inc(pool_step, 1)
                pool.wait_ge(pool_step, steps_done[0])

            nc.gpsimd.memset(xT_pad[:, :, 0:CHUNK], 0.0)
            nc.gpsimd.memset(akT[:, 0:CHUNK], 0.0)
            nc.gpsimd.memset(ones[:], 1.0)
            nc.gpsimd.memset(epsc, LN_EPS)
            nc.gpsimd.memset(mv1[:, :, :, P:P + 1], 1.0)
            nc.gpsimd.memset(bgu_raw, 0.0).then_inc(zero_done, 1)
            nc.gpsimd.dma_start(res[:], x.rearrange("(t p) n -> p t n", p=P)).then_inc(x_landed, 16)
            pool.wait_ge(zero_done, 1)
            for i in range(3):
                nc.gpsimd.dma_start(bgu_raw[N_EXP * i:N_EXP * (i + 1), :], b_gu).then_inc(bgu_landed, 16)
            nc.gpsimd.dma_start(router_w[:], w_router.rearrange("(k p) n -> p k n", p=P)).then_inc(router_landed, 16)
            nc.gpsimd.dma_start(brow[:], b_router.rearrange("(o n) -> o n", o=1).to_broadcast([P, N_EXP])).then_inc(router_landed, 16)
            pool.wait_ge(bgu_landed, 48)
            link(nc.gpsimd.tensor_copy(bgu3[:], bgu_raw))
            link(nc.gpsimd.tensor_tensor(bgu_rest, bgu_raw, bgu3[:], ALU.subtract))
            nc.gpsimd.tensor_copy(bgu3[N_EXP:2 * N_EXP, :], bgu_rest[N_EXP:2 * N_EXP, :])
            low = slice(2 * N_EXP, P)
            link(nc.gpsimd.tensor_copy(bgu3[low, :], bgu_rest[low, :]))
            link(nc.gpsimd.tensor_tensor(bgu_raw[low, :], bgu_rest[low, :], bgu3[low, :], ALU.subtract))
            nc.gpsimd.tensor_copy(bgu3[low, :], bgu_raw[low, :]).then_inc(bgu_split, 1)
            pool.wait_ge(mixer_done, 1)
            for i in range(3):
                if i:
                    pool.wait_ge(normed, TT * i)
                nc.gpsimd.dma_start(lnp[:], ln_p[i:i + 1].to_broadcast([P, 2 * D])).then_inc(ln_landed, 16)
                if i == 1:
                    wait_unit(pool, "oT1")
                    nc.gpsimd.dma_start(bdown, b_down).then_inc(bdown_landed, 16)

        @block.tensor
        def _(pe):
            mm = nc.tensor.matmul

            def open_unit(u):
                i = UNITS.index(u)
                if i > 1:
                    wait_taken(pe, UNITS[i - 2])
                return unit_banks(u)

            def close_unit(u, ins):
                ins.then_inc(pair_ready[PAIR_COUNT[u][0]], 1)

            def landed(piece):
                s, n = front_slot(piece)
                pe.wait_ge(slot_landed[s], 16 * n)
                return slot_view(s, SOURCE[piece][2])

            def project_T(u, rhs):
                banks = open_unit(u)
                w = landed(u)
                for m in range(4):
                    for k in range(KT):
                        ins = mm(banks[m // 2][:, (m % 2) * 256:(m % 2) * 256 + 256], w[:, k, m * P:(m + 1) * P], rhs[:, k, :],
                                 start=k == 0, stop=k == KT - 1)
                    if m == 3:
                        close_unit(u, ins)
                return ins

            def project(u, lhs, order=range(KT), late=None):
                banks = open_unit(u)
                w = landed(u)
                for t in range(TT):
                    for n, k in enumerate(order):
                        if late and t == 0 and n == KT // 2:
                            wait_taken(pe, late)
                        ins = mm(banks[t][:], lhs[:, k, t * P:(t + 1) * P], w[:, k, :], start=n == 0, stop=n == KT - 1)
                close_unit(u, ins)

            pe.wait_ge(xT_landed, 16)
            pe.wait_ge(gatew_landed, 16)
            pe.wait_ge(zero_done, 1)
            for t in range(TT):
                for k in range(KT):
                    ins = mm(psum[4][:, 8 * t:8 * t + 8], xk[:, k, t * P:(t + 1) * P], gate_w[:, k, :], start=k == 0, stop=k == KT - 1)
            ins.then_inc(gates_ready, 1)
            project_T("mq", xk)
            pe.wait_ge(logf_ready, 1)
            pe.wait_ge(early_landed, 16)
            mm(psum[4][:, 16:20], tri, logf[:, 0, :], start=True, stop=True)
            mm(psum[4][:, 20:24], ones[:], logf[:, 0, :], start=True, stop=False)
            mm(psum[4][:, 20:24], tri, logf[:, 1, :], start=False, stop=True).then_inc(cum_ready, 1)
            project_T("mk", xk)
            pe.wait_ge(late_landed, 16)
            pe.wait_ge(diag_ready, 2)
            mask4 = negm.rearrange("p (o s) -> p o s", o=1).to_broadcast([P, ML_H, P])
            pmask4 = posm.rearrange("p (o s) -> p o s", o=1).to_broadcast([P, ML_H, P])

            def v4(b):
                return psum[b][:].rearrange("p (h s) -> p h s", h=ML_H)

            mm(v4(5), ones[:], diag[:, 0], start=True, stop=False)
            mm(v4(5), ident, mask4, start=False, stop=True)
            mm(v4(6), ones[:], diag[:, 0], start=True, stop=True)
            mm(v4(7), ones[:], diag[:, 1], start=True, stop=False)
            mm(v4(7), ident, mask4, start=False, stop=True).then_inc(crow_ready, 1)
            project("mo", xk)
            pe.wait_ge(mdiag_ready, 2)
            mm(v4(5), ones[:], diag[:, 0], start=True, stop=False)
            mm(v4(5), ident, pmask4, start=False, stop=True)
            mm(v4(6), ones[:], diag[:, 1], start=True, stop=True)
            mm(v4(7), ones[:], diag[:, 1], start=True, stop=False)
            mm(v4(7), ident, pmask4, start=False, stop=True).then_inc(mrow_ready, 1)
            project("mv", xk)
            b0, b1 = open_unit("akav")
            w = landed("akav")
            for k in range(KT):
                mm(b0[:, 0:SEQ], w[:, k, 0:P], xk[:, k, :], start=k == 0, stop=k == KT - 1)
            for c in range(NCHUNK):
                for k in range(KT):
                    ins = mm(b1[:, c * P:(c + 1) * P], xT_pad[:, k, c * CHUNK:c * CHUNK + P], w[:, k, P:2 * P], start=k == 0, stop=k == KT - 1)
            close_unit("akav", ins)
            pe.wait_ge(qk_ready, 2)
            pe.wait_ge(decay_ready, 12)
            for b, (s, t) in enumerate(((0, 0), (0, 1), (1, 1))):
                for h in range(ML_H):
                    ins = mm(psum[5 + b][:, h * P:(h + 1) * P], mkT[:, h, s * P:(s + 1) * P], mqT[:, h, t * P:(t + 1) * P], start=True, stop=True)
            ins.then_inc(sraw_ready, 1)
            project_T("aq", xk)
            pe.wait_ge(wts_ready, 3)
            wait_taken(pe, "mv")
            for t in range(TT):
                for h in range(ML_H):
                    o = psum[4 + 2 * t + h // 2][:, (h % 2) * 129:(h % 2) * 129 + 129]
                    if t == 0:
                        ins = mm(o, decay[:, 0, h, :], mv1[:, 0, h, :], start=True, stop=True)
                    else:
                        mm(o, decay[:, 1, h, :], mv1[:, 0, h, :], start=True, stop=False)
                        ins = mm(o, decay[:, 2, h, :], mv1[:, 1, h, :], start=False, stop=True)
            ins.then_inc(num_ready, 1)
            wait_taken(pe, "aq")
            b = open_unit("rotq")
            for m in range(4):
                ins = mm(b[m // 2][:, (m % 2) * 256:(m % 2) * 256 + 256], rot, aqT[:, m, :], start=True, stop=True)
            close_unit("rotq", ins)
            wait_taken(pe, "akav")
            b = open_unit("rotk")
            close_unit("rotk", mm(b[0][:, 0:SEQ], rot, akT[:, CHUNK:], start=True, stop=True))
            pe.wait_ge(memT_landed, 16)
            project_T("ck0", memT_sb)
            pe.wait_ge(rope_ready, 2)
            pe.wait_ge(num_read, 8)
            for t in range(TT):
                for h in range(N_Q):
                    g = h // GROUP
                    for par in range(2):
                        c = 2 * t + par
                        o = psum[4 + 2 * t + h // 4][64 * par:64 * par + 64, (h % 4) * P:(h % 4) * P + P]
                        r = 64 * g
                        ins = mm(o, aqT[r:r + 64, h % 4, c * CHUNK:(c + 1) * CHUNK], akT[r:r + 64, c * CHUNK:c * CHUNK + P], start=True, stop=True)
                ins.then_inc(sco_ready, 1)
            project_T("ck1", memT_sb)
            for t in range(TT):
                pe.wait_ge(prob_ready, t + 1)
                for h in range(N_Q):
                    ins = nc.tensor.transpose(psum[4 + 2 * t + h // 4][:, (h % 4) * P:(h % 4) * P + P], prob[:, t, h, :], ident)
                ins.then_inc(pT_ready, 1)
            pe.wait_ge(hm_ready, 2)
            b = open_unit("hmT")
            for t in range(TT):
                for h in range(ML_H):
                    ins = nc.tensor.transpose(b[h // 2][:, (h % 2) * 256 + t * P:(h % 2) * 256 + t * P + P], hm[:, t, h, :], ident)
            close_unit("hmT", ins)
            pe.wait_ge(pT_read, 4)
            b = open_unit("pv")
            for m in range(4):
                for par in range(2):
                    h = 2 * m + par
                    g = h // GROUP
                    for c in range(NCHUNK):
                        ins = mm(b[m // 2][64 * par:64 * par + 64, (m % 2) * 256 + c * CHUNK:(m % 2) * 256 + (c + 1) * CHUNK],
                                 av[:, c, 64 * g:64 * g + 64], probT[:, c // 2, h, (c % 2) * CHUNK:(c % 2) * CHUNK + CHUNK], start=True, stop=True)
            close_unit("pv", ins)
            wait_taken(pe, "hmT")
            project("wo0", tT, order=(4, 5, 6, 7, 0, 1, 2, 3), late="pv")
            project("wo1", tT)
            project("cv0", memT_sb)
            project("cv1", memT_sb)

            def transpose_rows(u, t, done):
                pe.wait_ge(normed, done + t + 1)
                b = open_unit(u)
                for k in range(KT):
                    ins = nc.tensor.transpose(b[k // 4][:, (k % 4) * P:(k % 4) * P + P], res[:, t, k * P:(k + 1) * P], ident)
                close_unit(u, ins)

            transpose_rows("x1T0", 0, 0)
            transpose_rows("x1T1", 1, 0)
            wait_taken(pe, "x1T0")
            wait_taken(pe, "x1T1")
            project_T("cq0", tT)
            project_T("cq1", tT)
            for h in range(MEM_H):
                if h % 2 == 0:
                    wait_taken(pe, f"cq{h // 2}")
                    wait_taken(pe, f"ck{h // 2}")
                for t in range(TT):
                    for k in range(2):
                        ins = mm(psum[4 + h][:, t * N_MEM:(t + 1) * N_MEM], cqT[:, 2 * h + k, t * P:(t + 1) * P], memK[:, 2 * h + k, :],
                                 start=k == 0, stop=k == 1)
                ins.then_inc(cs_ready, 1)
            for h in range(MEM_H):
                pe.wait_ge(cprob_ready, h + 1)
                for t in range(TT):
                    for m in range(2):
                        ins = nc.tensor.transpose(psum[4 + h][:, (2 * m + t) * P:(2 * m + t + 1) * P], cP[:, h, t, m * P:(m + 1) * P], ident)
                ins.then_inc(cpT_ready, 1)
            wait_taken(pe, "cv0")
            wait_taken(pe, "cv1")
            for i, u in enumerate(("oT0", "oT1")):
                b = open_unit(u)
                for q in range(4):
                    m = 4 * i + q
                    pe.wait_ge(cpT_read, m // 2 + 1)
                    for k in range(2):
                        ins = mm(b[q // 2][:, (q % 2) * 256:(q % 2) * 256 + 256], memV[:, k, m * P:(m + 1) * P], cPT[:, k, m // 2, :],
                                 start=k == 0, stop=k == 1)
                close_unit(u, ins)
            wait_taken(pe, "oT0")
            w_halves = [landed("co0"), landed("co1")]
            for t in range(TT):
                banks = open_unit(f"co_t{t}")
                for i in range(2):
                    for k in range(KT):
                        if (t, i, k) == (0, 0, 4):
                            wait_taken(pe, "oT1")
                        ins = mm(banks[i][:], tT[:, k, t * P:(t + 1) * P], w_halves[i][:, k, :], start=k == 0, stop=k == KT - 1)
                close_unit(f"co_t{t}", ins)

            def keep_warm(n):
                for _ in range(n):
                    mm(psum[7][:, 0:SEQ], ident, late_c[:, 0:SEQ], start=True, stop=True)

            pe.wait_ge(router_landed, 32)
            for t in range(TT):
                transpose_rows(f"x2T{t}", t, TT)
                wait_taken(pe, f"x2T{t}")
                if t == 0:
                    b = open_unit("logit")
                for k in range(KT):
                    ins = mm(b[0][:, t * N_EXP:(t + 1) * N_EXP], tT[:, k, t * P:(t + 1) * P], router_w[:, k, :], start=k == 0, stop=k == KT - 1)
                if t == 0:
                    keep_warm(5)
            close_unit("logit", ins)
            keep_warm(5)
            pe.wait_ge(sel_ready, 1)
            mm(psum[4][:, 0:32], strict, selm[:, 0, :], start=True, stop=True)
            mm(psum[4][:, 32:64], ones[:], selm[:, 0, :], start=True, stop=False)
            mm(psum[4][:, 32:64], strict, selm[:, 1, :], start=False, stop=True)
            for t in range(TT):
                ins = mm(psum[4][0:N_EXP, 64:65], selm[:, t, :], ones[:, 0:1], start=t == 0, stop=t == 1)
            ins.then_inc(rank_ready, 1)
            keep_warm(2)
            pe.wait_ge(npass_ready, 1)
            mm(psum[4][:, 128:192], npass[0:N_EXP].to_broadcast([N_EXP, P]), e_both, start=True, stop=True)
            mm(psum[4][:, 192:193], e_rows[:, 0], npass[0:N_EXP], start=True, stop=True)
            mm(psum[4][:, 193:194], e_rows[:, 1], npass[0:N_EXP], start=True, stop=True).then_inc(base_ready, 1)
            for t in range(TT):
                ins = nc.tensor.transpose(psum[5][0:N_EXP, t * P:(t + 1) * P], gfull[:, t, :], ident)
            ins.then_inc(gT_ready, 1)
            keep_warm(1)
            pe.wait_ge(gT_read, 1)
            pe.wait_ge(bdown_landed, 16)
            wait_taken(pe, "logit")
            for t in range(TT):
                for d in range(2):
                    ins = mm(psum[2 * t + d][:], gT[:, t, :], bdown[:, d * 512:(d + 1) * 512], start=True, stop=False, skip_group_check=True)
            ins.then_inc(sums_open, 1)

            def gather():
                for t in range(TT):
                    for half in range(2):
                        ins = mm(psum[6][64 * half:64 * half + 64, :], hot[:, t, :], res[:, t, 512 * half:512 * half + 512],
                                 start=t == 0, stop=t == 1, skip_group_check=True)
                ins.then_inc(gath_done, 1)

            def transpose_gathered():
                for c in range(4):
                    ins = nc.tensor.transpose(psum[5][:, c * P:(c + 1) * P], xrows[:, c * P:(c + 1) * P], ident)
                ins.then_inc(xgT_done, 1)

            def scatter(end=False):
                for t in range(TT):
                    for d in range(2):
                        ins = mm(psum[2 * t + d][:], scatT[:, t * P:(t + 1) * P], ysb[:, d * 512:(d + 1) * 512], start=False, stop=end,
                                 skip_group_check=True)
                        if end:
                            ins.then_inc(scattered, 1)

            pe.wait_ge(hot_ready, 1)
            gather()
            pe.wait_ge(gT_read, 1)
            pe.wait_ge(xrows_ready, 1)
            transpose_gathered()
            pe.wait_ge(bgu_split, 1)
            passes = pe.alloc_register("passes")
            pe.reg_mov(passes, 0)
            pe.wait_ge(tables_ready, 1)

            def expert_pass(it, u):
                j = pe.snap(passes, min_val=0, max_val=MAX_PASSES)

                def chunk(c):
                    n = u * EXP_CHUNKS + c
                    s = RING_ORDER[n % RING]
                    turn = n // RING + 1
                    pe.wait_ge(slot_landed[s], it * (16 * UNROLL * EXP_CHUNKS // RING) + 16 * (front_loads[s] + turn))
                    return slot_words(s)

                pe.wait_ge(aT_ready, j + 1)
                pe.wait_ge(hotg_ready, j + 1)
                pe.wait_ge(xg_ready, j + 1)
                sel = osel.to_broadcast([P, SLOTS])
                for b in range(2):
                    for half in range(2):
                        mm(psum[4 + b][64 * half:64 * half + 64, :], sel, bgu3[:, (2 * b + half) * 512:(2 * b + half + 1) * 512],
                           start=True, stop=False, skip_group_check=True)
                for c in range(4):
                    w = chunk(c).rearrange("p (j n) -> p j n", j=2)
                    for kk in range(2):
                        k = 2 * c + kk
                        for b in range(2):
                            for half in range(2):
                                ins = mm(psum[4 + b][64 * half:64 * half + 64, :], xg[:, k // 4, k % 4, :], w[:, kk, (2 * b + half) * 512:(2 * b + half + 1) * 512],
                                         start=False, stop=k == KT - 1, skip_group_check=True)
                    ins.then_inc(chunk_used[c], 1)
                pe.wait_ge(y0_ready, j + 1)
                pe.wait_ge(y1_ready, j + 1)
                pe.wait_ge(scT_ready, j + 1)
                scatter()
                for t in range(TT):
                    ins = nc.tensor.transpose(psum[7][:, t * P:(t + 1) * P], hotg[:, t].rearrange("p f s -> p (f s)"), ident)
                ins.then_inc(scT_done, 1)
                pe.wait_ge(act_ready, j + 1)
                for c in range(4):
                    ins = nc.tensor.transpose(psum[4][:, c * P:(c + 1) * P], act[:, c * P:(c + 1) * P], ident)
                ins.then_inc(aT_done, 1)
                pe.wait_ge(hot_ready, j + 2)
                gather()
                pe.wait_ge(aT_ready, j + 2)
                pe.wait_ge(scT_ready, j + 2)
                for d in (1, 0):
                    wd = chunk(5 - d).rearrange("p (k n) -> p k n", k=KT)
                    if d == 0:
                        pe.wait_ge(xrows_ready, j + 2)
                        transpose_gathered()
                    for c in range(4):
                        for half in range(2):
                            ins = mm(psum[6 + d][64 * half:64 * half + 64, :], actT[:, c * P + half * 64:c * P + half * 64 + 64],
                                     wd[:, 4 * half + c, :], start=c == 0, stop=c == 3, skip_group_check=True)
                    ins.then_inc(chunk_used[5 - d], 1)
                pe.reg_add(passes, passes, 1)

            def all_passes(it, u):
                n_passes = pe.value_load(npass_i[0:1, bass.ds(it * UNROLL + u, 1)], min_val=1, max_val=SEQ // SLOTS)
                with pe.Fori(0, n_passes):
                    expert_pass(it, u)

            with pe.Fori(0, LOOPS) as it:
                for u in range(UNROLL):
                    all_passes(it, u)
            for u in range(N_EXP % UNROLL):
                all_passes(LOOPS, u)
            total = pe.snap(passes, min_val=1, max_val=MAX_PASSES)
            pe.wait_ge(y0_ready, total + 1)
            pe.wait_ge(y1_ready, total + 1)
            scatter(end=True)

        @block.scalar
        def _(act_e):
            steps_done = [0]
            af = nc.scalar.activation

            def link(ins):
                steps_done[0] += 1
                ins.then_inc(act_step, 1)
                act_e.wait_ge(act_step, steps_done[0])

            act_e.dma_start(early_c[:, E_PAR:E_W], early_par.rearrange("(o n) -> o n", o=1).to_broadcast([P, E_W - E_PAR])).then_inc(par_landed, 16)
            act_e.dma_start(early_c[:, 0:E_PAR], early).then_inc(early_landed, 16)
            act_e.dma_start(convp[:], conv_p).then_inc(conv_landed, 16)
            act_e.dma_start(late_c[:], late).then_inc(late_landed, 16)
            EXP_LN = "natural_log_exp_and_others"
            nc.scalar.preload_act_table_set(EXP_LN)
            act_e.wait_ge(exp1, 1)
            link(af(gneg, gneg, ACT.Exp))
            af(gln, gneg, ACT.Ln, bias=1.0).then_inc(ln1s, 1)
            wait_taken(act_e, "mq")
            af(sigq[:, 0:4], mqT, ACT.Sigmoid).then_inc(sig_ready, 1)
            wait_taken(act_e, "mk")
            af(sigq[:, 4:8], mkT, ACT.Sigmoid).then_inc(sig_ready, 1)
            wait_unit(act_e, "mo")
            for t in range(TT):
                af(sigo[:, t, :], unit_banks("mo")[t][:], ACT.Sigmoid).then_inc(taken["mo"], 1)
            act_e.wait_ge(mrow_ready, 1)
            nc.scalar.preload_act_table_set(EXP_LN)
            for b, s in enumerate((0, 0, 1)):
                for h in range(ML_H):
                    af(decay[:, b, h, :], psum[5 + b][:, h * P:(h + 1) * P], ACT.Exp, bias=csrc[:, s, h:h + 1], scale=-1.0).then_inc(decay_ready, 1)
            act_e.wait_ge(fm_ready, 1)
            af(dmin, fm, ACT.Exp, scale=-1.0).then_inc(dmin_ready, 1)
            wait_unit(act_e, "mv")
            for t in range(TT):
                af(mv1[:, t, :, 0:P], unit_banks("mv")[t][:].rearrange("p (h d) -> p h d", h=ML_H), ACT.Copy).then_inc(taken["mv"], 1)
            wait_unit(act_e, "akav")
            af(av, unit_banks("akav")[1][:].rearrange("p (c d) -> p c d", c=NCHUNK), ACT.Copy).then_inc(taken["akav"], 1)

            def take_T(u, dst, which=(0, 1)):
                wait_unit(act_e, u)
                for i in which:
                    af(dst[:, 2 * i:2 * i + 2, :], unit_banks(u)[i][:].rearrange("p (m t) -> p m t", m=2), ACT.Copy).then_inc(taken[u], 1)

            take_T("aq", aqT)
            act_e.wait_ge(bgu_split, 1)
            take_T("ck0", memK[:, 0:4])
            for t in range(TT):
                act_e.wait_ge(sco_ready, t + 1)
                for i in range(2):
                    af(prob[:, t, 4 * i:4 * i + 4, :], psum[4 + 2 * t + i][:].rearrange("p (h k) -> p h k", h=4), ACT.Copy,
                       scale=float(HD) ** -0.5).then_inc(sco_read, 1)
            act_e.wait_ge(hvar_ready, 1)
            link(af(lnt[:, 0:8], hag[:, :, 1], ACT.Ln, bias=epsc))
            af(hrs, lnt[:, 0:8], ACT.Exp, scale=-0.5).then_inc(hln_ready, 1)
            for t in range(TT):
                act_e.wait_ge(pmax_ready, t + 1)
                af(prob[:, t], prob[:, t], ACT.Exp).then_inc(pexp_ready, 1)
                af(asnk[:, t], asnk[:, t], ACT.Exp).then_inc(pexp_ready, 1)
            take_T("ck1", memK[:, 4:8])
            for t in range(TT):
                act_e.wait_ge(pT_ready, t + 1)
                for i in range(2):
                    af(probT[:, t, 4 * i:4 * i + 4, :], psum[4 + 2 * t + i][:].rearrange("p (h q) -> p h q", h=4), ACT.Copy).then_inc(pT_read, 1)
            take_T("pv", tT[:, 0:4])

            def take_rows(u, i):
                wait_unit(act_e, u)
                for t in range(TT):
                    af(memV[:, t, 512 * i:512 * i + 512], unit_banks(u)[t][:], ACT.Copy).then_inc(taken[u], 1)

            def rstd(first, t):
                act_e.wait_ge(var_ready, first + t + 1)
                link(af(lnt[:, 8 + t:9 + t], lag[:, t, 1:2], ACT.Ln, bias=epsc))
                af(lrs[:, t:t + 1], lnt[:, 8 + t:9 + t], ACT.Exp, scale=-0.5).then_inc(lnlog_ready, 1)

            def take_transposed(u, t, halves):
                wait_unit(act_e, u)
                for i in halves:
                    af(tT[:, 4 * i:4 * i + 4, t * P:(t + 1) * P], unit_banks(u)[i][:].rearrange("p (k t) -> p k t", k=4), ACT.Copy).then_inc(taken[u], 1)

            rstd(0, 0)
            rstd(0, 1)
            take_rows("cv0", 0)
            take_rows("cv1", 1)
            take_transposed("x1T0", 0, (1,))
            take_transposed("x1T1", 1, (1,))
            take_T("cq0", cqT[:, 0:4])
            take_T("cq1", cqT[:, 4:8])
            for h in range(MEM_H):
                act_e.wait_ge(cmax_ready, h + 1)
                for t in range(TT):
                    j = h * TT + t
                    af(cP[:, h, t, :], psum[4 + h][:, t * N_MEM:(t + 1) * N_MEM], ACT.Exp, bias=cmax[:, j:j + 1], scale=float(MEM_HD) ** -0.5,
                       accum_out=csum[:, j:j + 1]).then_inc(cexp_ready, 1)
            for h in range(MEM_H):
                act_e.wait_ge(cpT_ready, h + 1)
                af(cPT[:, :, h, :], psum[4 + h][:].rearrange("p (m t) -> p m t", m=2), ACT.Copy).then_inc(cpT_read, 1)
            take_T("oT0", tT[:, 0:4])
            take_T("oT1", tT[:, 4:8])
            rstd(TT, 0)
            take_transposed("x2T0", 0, (0, 1))
            rstd(TT, 1)
            take_transposed("x2T1", 1, (1,))
            act_e.wait_ge(rmax_ready, 1)
            for t in range(TT):
                af(eg[:, t, :], top8[:, t, 0:TOP_K], ACT.Exp, bias=rmax[:, t:t + 1], accum_out=rsum[:, t:t + 1]).then_inc(rexp_ready, 1)
            act_e.wait_ge(gT_ready, 1)
            af(gT, psum[5][0:N_EXP, 0:SEQ].rearrange("p (t n) -> p t n", t=TT), ACT.Copy).then_inc(gT_read, 1)
            act_e.wait_ge(gath_done, 1)
            af(xrows, psum[6][:], ACT.Copy).then_inc(xrows_ready, 1)
            act_e.wait_ge(xgT_done, 1)
            af(m0[:, 0:512], psum[5][:], ACT.Copy).then_inc(xg_ready, 1)
            act_e.wait_ge(tables_ready, 1)
            total = act_e.value_load(cum_i[0:1, N_EXP - 1:N_EXP], min_val=1, max_val=MAX_PASSES)
            nc.scalar.preload_act_table(ACT.Sigmoid)
            with act_e.Fori(0, total) as j:
                act_e.wait_ge(gcl_ready, j + 1)
                af(sgm, gcl, ACT.Sigmoid, scale=SWIGLU_ALPHA).then_inc(sgm_ready, 1)
                act_e.wait_ge(scT_done, j + 1)
                af(scatT, psum[7][:, 0:SEQ], ACT.Copy).then_inc(scT_ready, 1)
                act_e.wait_ge(gath_done, j + 2)
                af(xrows, psum[6][:], ACT.Copy).then_inc(xrows_ready, 1)
                act_e.wait_ge(xgT_done, j + 2)
                af(m0[:, 0:512], psum[5][:], ACT.Copy).then_inc(xg_ready, 1)
                act_e.wait_ge(chunk_used[5], j + 1)
                af(ysb[:, 0:512], psum[6][:], ACT.Copy).then_inc(y0_ready, 1)
            nc.scalar.preload_act_table_set(EXP_LN)
            rstd(2 * TT, 0)
            rstd(2 * TT, 1)

        @block.vector
        def _(dve):
            steps_done = [0]
            v = nc.vector

            def link(ins):
                steps_done[0] += 1
                ins.then_inc(dve_step, 1)
                dve.wait_ge(dve_step, steps_done[0])

            def bc(ap, shape):
                return ap.to_broadcast(shape)

            dve.wait_ge(par_landed, 16)
            dve.wait_ge(gates_ready, 1)
            link(v.tensor_tensor(gi, psum[4][:, 0:16].rearrange("p (t g) -> p t g", t=TT),
                                 bc(bgate.rearrange("p (o g) -> p o g", o=1), [P, TT, 8]), ALU.add))
            link(v.tensor_scalar(gneg, gi[:, :, 4:8], -1.0, None, ALU.mult))
            v.tensor_tensor(gneg, gneg, gi[:, :, 4:8], ALU.min).then_inc(exp1, 1)
            dve.wait_ge(ln1s, 1)
            v.scalar_tensor_tensor(out=logf, in0=gi[:, :, 4:8], scalar=0.0, in1=gln, op0=ALU.min, op1=ALU.subtract).then_inc(logf_ready, 1)

            def conv(u, dst, m0):
                dve.wait_ge(conv_landed, 16)
                wait_unit(dve, u)
                src = [unit_banks(u)[m // 2][:, (m % 2) * 256:(m % 2) * 256 + 256] for m in range(4)]
                base = steps_done[0]
                for back in range(CONV_W):
                    for m in range(4):
                        tap = convp[:, m0 + m, CONV_W - 1 - back:CONV_W - back]
                        if back:
                            dve.wait_ge(dve_step, base + 4 * (back - 1) + m + 1)
                            ins = v.scalar_tensor_tensor(out=dst[:, m, back:], in0=src[m][:, 0:SEQ - back], scalar=tap,
                                                         in1=dst[:, m, back:], op0=ALU.mult, op1=ALU.add)
                        else:
                            ins = v.tensor_scalar(dst[:, m, :], src[m], tap, convp[:, m0 + m, CONV_W:CONV_W + 1], ALU.mult, ALU.add)
                        if back < CONV_W - 1:
                            ins.then_inc(dve_step, 1)
                            steps_done[0] += 1
                        else:
                            ins.then_inc(taken[u], 1)

            conv("mq", mqT, 0)
            dve.wait_ge(late_landed, 16)
            dve.wait_ge(cum_ready, 1)
            link(v.tensor_copy(cumf, psum[4][:, 16:24].rearrange("p (t h) -> p t h", t=TT)))
            link(v.tensor_tensor(csrc, gi[:, :, 0:4], cumf, ALU.subtract))
            idb = bc(ident.rearrange("p (o s) -> p o s", o=1), [P, ML_H, P])

            def diagonals(values, ready):
                for t in range(TT):
                    v.tensor_tensor(diag[:, t], idb, bc(values[:, t].rearrange("p (h o) -> p h o", o=1), [P, ML_H, P]), ALU.mult).then_inc(ready, 1)

            diagonals(csrc, diag_ready)
            conv("mk", mkT, 4)
            dve.wait_ge(crow_ready, 1)
            for b in range(3):
                ins = v.reduce_max(m3[:, b, :], psum[5 + b][:].rearrange("p (h s) -> p h s", h=ML_H), AX_X)
            link(ins)
            link(v.tensor_tensor(m3[:, 1, :], m3[:, 1, :], m3[:, 2, :], ALU.max))
            link(v.tensor_scalar(mrun, m3[:, 0:2, :], 0.0, None, ALU.max))
            diagonals(mrun, mdiag_ready)
            v.tensor_tensor(fm, cumf, mrun, ALU.add).then_inc(fm_ready, 1)
            for i, (dst) in enumerate((mqT, mkT)):
                dve.wait_ge(sig_ready, i + 1)
                v.tensor_tensor(dst, dst, sigq[:, 4 * i:4 * i + 4], ALU.mult).then_inc(qk_ready, 1)
            wait_taken(dve, "mo")
            for t in range(TT):
                ins = v.tensor_tensor(sigo[:, t, :], sigo[:, t, :], normw, ALU.mult)
            link(ins)
            wait_unit(dve, "akav")
            v.tensor_copy(akT[:, CHUNK:], unit_banks("akav")[0][:, 0:SEQ]).then_inc(taken["akav"], 1)
            dve.wait_ge(sraw_ready, 1)
            for b in range(3):
                v.scalar_tensor_tensor(out=decay[:, b], in0=psum[5 + b][:].rearrange("p (h t) -> p h t", h=ML_H), scalar=float(P) ** -0.5,
                                       in1=decay[:, b], op0=ALU.mult, op1=ALU.mult).then_inc(wts_ready, 1)
            dve.wait_ge(num_ready, 1)
            dve.wait_ge(dmin_ready, 1)
            for j in range(4):
                ins = v.tensor_copy(den[:, j // 2, 2 * (j % 2):2 * (j % 2) + 2], psum[4 + j][:, 0:258].rearrange("p (h d) -> p h d", h=2)[:, :, P])
            link(ins)
            link(v.scalar_tensor_tensor(out=den, in0=den, scalar=-1.0, in1=den, op0=ALU.mult, op1=ALU.max))
            link(v.tensor_tensor(den, den, dmin, ALU.max))
            link(v.reciprocal(den, den))
            def scale_numerators(t):
                for h in range(ML_H):
                    v.tensor_scalar(hm[:, t, h, :], psum[4 + 2 * t + h // 2][:, (h % 2) * 129:(h % 2) * 129 + P], den[:, t, h:h + 1], None,
                                    ALU.mult).then_inc(num_read, 1)
            scale_numerators(0)
            cos2 = bc(cosT.rearrange("p (o t) -> p o t", o=1), [P, 2, SEQ])
            sin2 = bc(sinT.rearrange("p (o t) -> p o t", o=1), [P, 2, SEQ])
            wait_unit(dve, "rotq")
            for i in range(2):
                v.tensor_tensor(qrot[:, 2 * i:2 * i + 2], unit_banks("rotq")[i][:].rearrange("p (m t) -> p m t", m=2), sin2, ALU.mult).then_inc(taken["rotq"], 1)
            scale_numerators(1)
            wait_unit(dve, "rotk")
            v.tensor_tensor(akrot[:], unit_banks("rotk")[0][:, 0:SEQ], sinT, ALU.mult).then_inc(taken["rotk"], 1)
            for i in range(2):
                v.tensor_tensor(aqT[:, 2 * i:2 * i + 2], aqT[:, 2 * i:2 * i + 2], cos2, ALU.mult)
            link(v.tensor_tensor(akT[:, CHUNK:], akT[:, CHUNK:], cosT, ALU.mult))
            wait_taken(dve, "rotq")
            wait_taken(dve, "rotk")
            v.tensor_tensor(aqT, aqT, qrot, ALU.add).then_inc(rope_ready, 1)
            v.tensor_tensor(akT[:, CHUNK:], akT[:, CHUNK:], akrot[:], ALU.add).then_inc(rope_ready, 1)
            dve.wait_ge(num_read, 8)
            for j in range(8):
                ins = v.bn_stats(hst[:, j, :], hm[:, j // ML_H, j % ML_H, :])
            link(ins)
            for j in range(8):
                ins = v.bn_aggr(hag[:, j, :], hst[:, j, :])
            ins.then_inc(hvar_ready, 1)
            dve.wait_ge(hvar_ready, 1)

            def newton(y, var, n, tmp):
                link(v.tensor_tensor(tmp, y, y, ALU.mult))
                link(v.scalar_tensor_tensor(out=tmp, in0=var, scalar=epsc, in1=tmp, op0=ALU.add, op1=ALU.mult))
                link(v.tensor_scalar(tmp, tmp, -0.5, 1.5, ALU.mult, ALU.add))
                return v.tensor_tensor(y, y, tmp, ALU.mult)

            def window_softmax(t):
                dve.wait_ge(sco_read, 2 * t + 2)
                if t == 0:
                    link(v.memset(prob[0:CHUNK, 0, :, 0:CHUNK], -BIG))
                link(v.reduce_max(amax[:, t], prob[:, t], AX_X))
                link(v.tensor_tensor(amax[:, t], amax[:, t], sinks, ALU.max))
                v.tensor_tensor(asnk[:, t], sinks, amax[:, t], ALU.subtract)
                v.tensor_tensor(prob[:, t], prob[:, t], bc(amax[:, t].rearrange("p (h o) -> p h o", o=1), [P, N_Q, P]), ALU.subtract).then_inc(pmax_ready, 1)

            window_softmax(0)
            dve.wait_ge(hln_ready, 1)
            link(newton(hrs, hag[:, :, 1], 8, nwt[:, 0:8]))
            for j in range(8):
                ins = v.tensor_scalar(hm[:, j // ML_H, j % ML_H, :], hm[:, j // ML_H, j % ML_H, :], hag[:, j, 0:1], hrs[:, j:j + 1], ALU.subtract, ALU.mult)
            link(ins)
            for t in range(TT):
                hv = hm[:, t].rearrange("p h d -> p (h d)")
                v.tensor_tensor(hv, hv, sigo[:, t, :], ALU.mult).then_inc(hm_ready, 1)
            window_softmax(1)
            for t in range(TT):
                dve.wait_ge(pexp_ready, 2 * t + 2)
                link(v.reduce_sum(asum[:, t], prob[:, t], AX_X))
                link(v.tensor_tensor(asum[:, t], asum[:, t], asnk[:, t], ALU.add))
                link(v.reciprocal(asum[:, t], asum[:, t]))
                v.tensor_tensor(prob[:, t], prob[:, t], bc(asum[:, t].rearrange("p (h o) -> p h o", o=1), [P, N_Q, P]), ALU.mult).then_inc(prob_ready, 1)
            wait_unit(dve, "hmT")
            for i in range(2):
                v.tensor_copy(tT[:, 4 + 2 * i:6 + 2 * i, :], unit_banks("hmT")[i][:].rearrange("p (m t) -> p m t", m=2)).then_inc(taken["hmT"], 1)
            wait_unit(dve, "pv")
            v.memset(nwt[:, 15:16], 0.0).then_inc(mixer_done, 1)

            def statistics(t):
                for i in range(2):
                    ins = v.bn_stats(lst[:, t, i, :], res[:, t, 512 * i:512 * i + 512])
                link(ins)
                v.bn_aggr(lag[:, t, :], lst[:, t].rearrange("p c s -> p (c s)")).then_inc(var_ready, 1)

            def normalise(t, first, ready):
                dve.wait_ge(ln_landed, 16 * (first // TT + 1))
                dve.wait_ge(var_ready, first + t + 1)
                link(v.scalar_tensor_tensor(out=res[:, t, :], in0=res[:, t, :], scalar=lag[:, t, 0:1], in1=lnp[:, 0:D], op0=ALU.subtract, op1=ALU.mult))
                dve.wait_ge(lnlog_ready, first + t + 1)
                link(newton(lrs[:, t:t + 1], lag[:, t, 1:2], 1, nwt[:, 8 + t:9 + t]))
                v.scalar_tensor_tensor(out=res[:, t, :], in0=res[:, t, :], scalar=lrs[:, t:t + 1], in1=lnp[:, D:2 * D], op0=ALU.mult,
                                       op1=ALU.add).then_inc(ready, 1)

            def add_to_residual(t, i, bank):
                c = slice(512 * i, 512 * i + 512)
                return v.scalar_tensor_tensor(out=res[:, t, c], in0=res[:, t, c], scalar=DEEPNORM_ALPHA, in1=bank[:], op0=ALU.mult, op1=ALU.add)

            def take_transposed(u, t):
                wait_unit(dve, u)
                v.tensor_copy(tT[:, 0:4, t * P:(t + 1) * P], unit_banks(u)[0][:].rearrange("p (k t) -> p k t", k=4)).then_inc(taken[u], 1)

            dve.wait_ge(x_landed, 16)
            for i, u in enumerate(("wo0", "wo1")):
                wait_unit(dve, u)
                for t in range(TT):
                    add_to_residual(t, i, unit_banks(u)[t]).then_inc(taken[u], 1)
            wait_taken(dve, "wo0")
            wait_taken(dve, "wo1")
            for t in range(TT):
                statistics(t)
            for t in range(TT):
                normalise(t, 0, normed)
            take_transposed("x1T0", 0)
            take_transposed("x1T1", 1)
            for h in range(MEM_H):
                dve.wait_ge(cs_ready, h + 1)
                j = h * TT
                link(v.reduce_max(cmax[:, j:j + 2], psum[4 + h][:].rearrange("p (t m) -> p t m", t=TT), AX_X))
                v.tensor_scalar(cmax[:, j:j + 2], cmax[:, j:j + 2], -float(MEM_HD) ** -0.5, None, ALU.mult).then_inc(cmax_ready, 1)
            for h in range(MEM_H):
                dve.wait_ge(cexp_ready, TT * (h + 1))
                j = h * TT
                link(v.reciprocal(csum[:, j:j + 2], csum[:, j:j + 2]))
                v.tensor_tensor(cP[:, h], cP[:, h], bc(csum[:, j:j + 2].rearrange("p (t o) -> p t o", o=1), [P, TT, N_MEM]), ALU.mult).then_inc(cprob_ready, 1)
            for t in range(TT):
                u = f"co_t{t}"
                wait_unit(dve, u)
                for i in range(2):
                    add_to_residual(t, i, unit_banks(u)[i]).then_inc(taken[u], 1)
                wait_taken(dve, u)
                statistics(t)
                normalise(t, TT, normed)
            take_transposed("x2T1", 1)
            v.memset(ysb[:, 0:512], 0.0).then_inc(y0_ready, 1)
            v.memset(ysb[:, 512:1024], 0.0).then_inc(y1_ready, 1)
            v.memset(scatT, 0.0).then_inc(scT_ready, 1)

            dve.wait_ge(router_landed, 32)
            wait_unit(dve, "logit")
            v.tensor_tensor(logits, unit_banks("logit")[0][:, 0:TT * N_EXP].rearrange("p (t e) -> p t e", t=TT),
                            bc(brow[:].rearrange("p (o e) -> p o e", o=1), [P, TT, N_EXP]), ALU.add).then_inc(taken["logit"], 1)
            wait_taken(dve, "logit")
            for t in range(TT):
                ins = v.max(top8[:, t, :], logits[:, t, :])
            link(ins)
            v.tensor_scalar(rmax, top8[:, :, 0], -1.0, None, ALU.mult).then_inc(rmax_ready, 1)
            for t in range(TT):
                ins = v.max_index(idx8[:, t, :], top8[:, t, :], logits[:, t, :])
            link(ins)
            link(v.tensor_copy(idx4.rearrange("p (t k) -> p t k", t=TT), idx8[:, :, 0:TOP_K]))
            link(v.tensor_tensor(onehot, bc(iota[:, 0:N_EXP].rearrange("p (o e) -> p o e", o=1), [P, 8, N_EXP]),
                                 bc(idx4.rearrange("p (j o) -> p j o", o=1), [P, 8, N_EXP]), ALU.is_equal))
            for t in range(TT):
                ins = v.reduce_sum(selm[:, t, :], onehot[:, 4 * t:4 * t + 4].rearrange("p k e -> p e k"), AX_X)
            ins.then_inc(sel_ready, 1)
            dve.wait_ge(rexp_ready, 2)
            link(v.reciprocal(rsum, rsum))
            link(v.tensor_tensor(gate.rearrange("p (t k) -> p t k", t=TT), eg, bc(rsum.rearrange("p (t o) -> p t o", o=1), [P, TT, TOP_K]), ALU.mult))
            link(v.tensor_tensor(tmp8, onehot, bc(gate.rearrange("p (j o) -> p j o", o=1), [P, 8, N_EXP]), ALU.mult))
            for t in range(TT):
                ins = v.reduce_sum(gfull[:, t, :], tmp8[:, 4 * t:4 * t + 4].rearrange("p k e -> p e k"), AX_X)
            link(ins)
            dve.wait_ge(rank_ready, 1)
            for i in range(3):
                ins = v.tensor_scalar(steps[0:N_EXP, i:i + 1], psum[4][0:N_EXP, 64:65], float(SLOTS * (i + 1)), None, ALU.is_gt)
            link(ins)
            link(v.reduce_sum(npass[0:N_EXP], steps[0:N_EXP, 0:3], AX_X))
            v.tensor_scalar(npass[0:N_EXP], npass[0:N_EXP], 1.0, None, ALU.add).then_inc(npass_ready, 1)
            dve.wait_ge(npass_ready, 1)
            dve.wait_ge(base_ready, 1)
            v.tensor_copy(first, psum[4][:, 192:193])
            v.tensor_copy(last, psum[4][:, 193:194])
            link(v.tensor_copy(cumrow, psum[4][:, 128:192]))
            v.tensor_copy(cum_i[0:1, :], cumrow[0:1, N_EXP:2 * N_EXP])
            v.tensor_tensor(npass_i[0:1, :], cumrow[0:1, N_EXP:2 * N_EXP], cumrow[0:1, 0:N_EXP], ALU.subtract).then_inc(tables_ready, 1)
            rank = psum[4][:, 0:64].rearrange("p (t e) -> p t e", t=TT)
            link(v.scalar_tensor_tensor(out=dest, in0=bc(cumrow[:, 0:N_EXP].rearrange("p (o e) -> p o e", o=1), [P, TT, N_EXP]), scalar=float(SLOTS),
                                        in1=rank, op0=ALU.mult, op1=ALU.add))
            for t in range(TT):
                ins = v.tensor_tensor(tmp8[:, 4 * t:4 * t + 4], onehot[:, 4 * t:4 * t + 4], bc(dest[:, t:t + 1, :], [P, TOP_K, N_EXP]), ALU.mult)
            link(ins)
            link(v.reduce_sum(rel, tmp8, AX_X))

            eqf = eq.rearrange("p t k s -> p (t k) s")
            gqf = gq.rearrange("p t k s -> p (t k) s")

            def mark_tokens(chain):
                chain(v.tensor_tensor(eqf, bc(iota.rearrange("p (o s) -> p o s", o=1), [P, 8, SLOTS]), bc(rel.rearrange("p (j o) -> p j o", o=1), [P, 8, SLOTS]),
                                      ALU.is_equal))
                v.tensor_scalar(rel, rel, -float(SLOTS), None, ALU.add)
                for t in range(TT):
                    ins = v.reduce_sum(hot[:, t, :], eq[:, t].rearrange("p k s -> p s k"), AX_X)
                ins.then_inc(hot_ready, 1)

            def mark_gates(chain):
                chain(v.tensor_tensor(gqf, eqf, bc(gate.rearrange("p (j o) -> p j o", o=1), [P, 8, SLOTS]), ALU.mult))
                for t in range(TT):
                    for f in range(2):
                        v.reduce_sum(hotg[:, t, f, :], gq[:, t].rearrange("p k s -> p s k"), AX_X)
                chain(v.tensor_scalar(began, first, 0.0, None, ALU.is_le))
                v.scalar_tensor_tensor(out=osel, in0=last, scalar=0.0, in1=began, op0=ALU.is_gt, op1=ALU.mult).then_inc(hotg_ready, 1)
                v.tensor_scalar(first, first, -1.0, None, ALU.add)
                chain(v.tensor_scalar(last, last, -1.0, None, ALU.add))

            mark_tokens(link)
            mark_gates(link)
            dve.wait_ge(gT_read, 1)
            v.memset(nwt[:, 14:15], 0.0).then_inc(aT_ready, 1)
            total = dve.value_load(cum_i[0:1, N_EXP - 1:N_EXP], min_val=1, max_val=MAX_PASSES)
            STEPS = 6
            loop_base = steps_done[0]
            with dve.Fori(0, total) as j:
                count = [0]

                def chain(ins):
                    count[0] += 1
                    ins.then_inc(dve_step, 1)
                    dve.wait_ge(dve_step, j * STEPS + (loop_base + count[0]))

                dve.wait_ge(gath_done, j + 1)
                mark_tokens(chain)
                dve.wait_ge(chunk_used[3], j + 1)
                v.tensor_scalar(gcl, psum[4][:], LIMIT, None, ALU.min).then_inc(gcl_ready, 1)
                chain(v.tensor_scalar(ucl, psum[5][:], LIMIT, -LIMIT, ALU.min, ALU.max))
                dve.wait_ge(sgm_ready, j + 1)
                chain(v.tensor_tensor(sgm, sgm, gcl, ALU.mult))
                v.scalar_tensor_tensor(out=act, in0=ucl, scalar=1.0, in1=sgm, op0=ALU.add, op1=ALU.mult).then_inc(act_ready, 1)
                dve.wait_ge(aT_done, j + 1)
                v.tensor_copy(actT, psum[4][:]).then_inc(aT_ready, 1)
                dve.wait_ge(scT_done, j + 1)
                mark_gates(chain)
                dve.wait_ge(chunk_used[4], j + 1)
                v.tensor_copy(ysb[:, 512:1024], psum[7][:]).then_inc(y1_ready, 1)
                assert count[0] == STEPS
            tail = [0]

            def link(ins):
                tail[0] += 1
                ins.then_inc(tail_step, 1)
                dve.wait_ge(tail_step, tail[0])

            for t in range(TT):
                for i in range(2):
                    dve.wait_ge(scattered, 2 * t + i + 1)
                    add_to_residual(t, i, psum[2 * t + i]).then_inc(sum_ready, 1)
                dve.wait_ge(sum_ready, 2 * t + 2)
                statistics(t)
            for t in range(TT):
                normalise(t, 2 * TT, final_ready)


def tables():
    import numpy as np

    f = np.float32
    inv = (f(1.0) / (f(10000.0) ** (np.arange(0, HD, 2, dtype=f) / f(HD)))).astype(f)
    ang = np.arange(SEQ, dtype=f)[:, None] * inv[None, :]
    ang = np.concatenate([ang, ang], axis=-1).T
    i = np.arange(P)
    early = np.zeros((P, E_PAR), f)
    early[:, E_TRI:E_TRI + P] = i[:, None] <= i[None, :]
    rot = np.zeros((P, P), f)
    for d in range(P):
        if d % HD < HD // 2:
            rot[d + HD // 2, d] = -1.0
        else:
            rot[d - HD // 2, d] = 1.0
    early[:, E_ROT:E_ROT + P] = rot
    early[:, E_COS:E_COS + SEQ] = np.cos(np.concatenate([ang, ang], axis=0))
    early[:, E_SIN:E_SIN + SEQ] = np.sin(np.concatenate([ang, ang], axis=0))
    early[:, E_NEG:E_NEG + P] = np.where(i[None, :] > i[:, None], -BIG, 0.0)
    early[:, E_POS:E_POS + P] = np.where(i[:, None] > i[None, :], BIG, 0.0)
    late = np.zeros((P, L_W), f)
    late[:, L_ID:L_ID + P] = np.eye(P)
    late[:, L_STRICT:L_STRICT + P] = i[:, None] < i[None, :]
    late[:, L_IOTA:L_IOTA + SLOTS] = np.arange(SLOTS)
    e = np.arange(N_EXP)
    late[:N_EXP, L_ESTRICT:L_ESTRICT + N_EXP] = e[:, None] < e[None, :]
    late[:N_EXP, L_EINCL:L_EINCL + N_EXP] = e[:, None] <= e[None, :]
    late[:N_EXP, L_ROWS:L_ROWS + P] = e[:, None] < np.tile(e, 4)[None, :]
    late[:N_EXP, L_ROWS + P:L_ROWS + 2 * P] = e[:, None] <= np.tile(e, 4)[None, :]
    return early, late


def kernel(x, mem, w_in, conv_w, conv_b, attn_sinks, b_igate, b_fgate, mlstm_norm_w, w_out, ln1_g, ln1_b, w_cq, w_ck, w_cv, w_co,
           ln2_g, ln2_b, w_router, b_router, w_gu, b_gu, w_down, b_down, ln3_g, ln3_b):
    import numpy as np
    import concourse.bacc as bacc
    from concourse.bass_utils import run_bass_kernel_spmd

    early, late = tables()
    lay = np.ascontiguousarray
    conv = np.concatenate([conv_w[0], conv_b], axis=0)
    aq = w_in[0][:, :C_AK].reshape(D, N_KV, GROUP, HD).transpose(0, 2, 1, 3).reshape(D, C_AK)
    w_in = np.concatenate([aq, w_in[0][:, C_AK:]], axis=1)
    arrays = {
        "x": lay(x[0]), "xT": lay(x[0].T), "memT": lay(mem[0].T), "w_in": lay(w_in),
        "conv_p": lay(conv.reshape(CONV_W + 1, 8, P).transpose(2, 1, 0)),
        "early": early,
        "early_par": np.concatenate([attn_sinks[0], b_igate[0], b_fgate[0], mlstm_norm_w[0]]),
        "late": late, "w_out": lay(w_out[0]),
        "ln_p": np.stack([np.concatenate([ln1_g[0], ln1_b[0]]), np.concatenate([ln2_g[0], ln2_b[0]]), np.concatenate([ln3_g[0], ln3_b[0]])]),
        "w_cq": lay(w_cq[0]), "w_ck": lay(w_ck[0]), "w_cv": lay(w_cv[0]), "w_co": lay(w_co[0]),
        "w_router": lay(w_router[0]), "b_router": lay(b_router[0]), "w_gu": lay(w_gu[0]), "b_gu": lay(b_gu[0]),
        "w_down": lay(w_down[0]), "b_down": lay(b_down[0]),
    }
    arrays = {f"in_{k}": np.asarray(a) for k, a in arrays.items()}
    nc = bacc.Bacc("TRN2", target_bir_lowering=False, num_devices=1)
    args = [nc.dram_tensor(n, a.shape, mybir.dt.from_np(a.dtype), kind="ExternalInput").ap() for n, a in arrays.items()]
    args.append(nc.dram_tensor("out", (SEQ, D), F32, kind="ExternalOutput").ap())
    layer_program(nc, *args)
    r = run_bass_kernel_spmd(nc, [arrays], core_ids=[0])
    return r.results[0]["out"].reshape(1, SEQ, D)
```
